# Optimizing a Trainium2 kernel written in Bass

```python
import jax, jax.numpy as jnp
from jax import lax
import numpy as np

D_MODEL = 1024
BATCH = 1
SEQ = 4096
DEPTH = 1
DEC_BATCH = 8
DEC_SEQ = 8
PAST_LEN = 1024
PAGE_SIZE = 128

HEAD_DIM = 64
ROT_DIM = HEAD_DIM // 4
ROPE_THETA = 500000.0
EPS = 1e-6
A_HEADS = 6
A_KV_HEADS = 2
DILATED_PATTERNS = ((128, 1), (512, 4), (2048, 16))
WIN_MAX = max(w for w, _ in DILATED_PATTERNS)
B_HEADS = 6
B_KV_HEADS = 2
IDX_HEADS = 8
IDX_DIM = 64
TOPK_MAX = 256
Q_BLOCK = 128
C_HEADS = 4
MEM_LEN = 256

A_Q = A_HEADS * HEAD_DIM
A_KV = A_KV_HEADS * HEAD_DIM
B_Q = B_HEADS * HEAD_DIM
B_KV = B_KV_HEADS * HEAD_DIM
C_Q = C_HEADS * HEAD_DIM
MIX_WIDTH = A_Q + B_Q + C_Q
SPLIT_SIZES = (A_Q, A_KV, A_KV, A_Q, B_Q, B_KV, B_KV, IDX_HEADS * IDX_DIM, IDX_DIM, IDX_HEADS, B_Q, C_Q, C_Q)
SPLIT_POINTS = tuple(int(v) for v in np.cumsum(SPLIT_SIZES)[:-1])
IN_WIDTH = sum(SPLIT_SIZES)

kernel_name = 'hymba_dilated_dsa_memory_step'

def _rmsnorm(x, g):
    xf = x.astype(jnp.float32)
    y = xf * lax.rsqrt(jnp.mean(xf * xf, axis=-1, keepdims=True) + EPS)
    return (y * g.astype(jnp.float32)).astype(x.dtype)

def _rope(x, pos):
    half = ROT_DIM // 2
    inv = jnp.power(ROPE_THETA, -jnp.arange(half, dtype=jnp.float32) * 2.0 / ROT_DIM)
    ang = pos.astype(jnp.float32)[:, None] * inv[None, :]
    cos = jnp.cos(ang)[:, None, :]
    sin = jnp.sin(ang)[:, None, :]
    xf = x.astype(jnp.float32)
    x1, x2, rest = xf[..., :half], xf[..., half:ROT_DIM], xf[..., ROT_DIM:]
    return jnp.concatenate([x1 * cos - x2 * sin, x2 * cos + x1 * sin, rest], axis=-1).astype(x.dtype)

def _branch_inputs(x, pos, g_in, w_in):
    N, T, _ = x.shape
    z = _rmsnorm(x, g_in) @ w_in
    aq, ak, av, ag, bq, bk, bv, iq, ik, iw, bg, cq, cg = jnp.split(z, SPLIT_POINTS, axis=-1)
    aq = _rope(aq.reshape(N, T, A_HEADS, HEAD_DIM), pos)
    ak = _rope(ak.reshape(N, T, A_KV_HEADS, HEAD_DIM), pos)
    av = av.reshape(N, T, A_KV_HEADS, HEAD_DIM)
    bq = _rope(bq.reshape(N, T, B_HEADS, HEAD_DIM), pos)
    bk = _rope(bk.reshape(N, T, B_KV_HEADS, HEAD_DIM), pos)
    bv = bv.reshape(N, T, B_KV_HEADS, HEAD_DIM)
    iq = _rope(iq.reshape(N, T, IDX_HEADS, IDX_DIM), pos)
    ik = _rope(ik.reshape(N, T, 1, IDX_DIM), pos)[:, :, 0]
    cq = cq.reshape(N, T, C_HEADS, HEAD_DIM)
    return aq, ak, av, ag, bq, bk, bv, iq, ik, iw, bg, cq, cg

def _dilated_prompt(q, k, v, dil, n_back):
    f32 = jnp.float32
    N, S = q.shape[:2]
    G = A_HEADS // A_KV_HEADS
    blk = n_back
    span = dil * blk
    s_pad = -(-S // span) * span
    nb = s_pad // span

    def to_sub(a):
        a = jnp.pad(a.astype(f32), ((0, 0), (0, s_pad - S), (0, 0), (0, 0)))
        a = a.reshape(N, s_pad // dil, dil, a.shape[2], HEAD_DIM).swapaxes(1, 2)
        return a.reshape(N, dil, nb, blk, a.shape[3], HEAD_DIM)

    def band(a):
        a = to_sub(a)
        prev = jnp.pad(a, ((0, 0), (0, 0), (1, 0), (0, 0), (0, 0), (0, 0)))[:, :, :-1]
        return jnp.concatenate([prev, a], axis=3)

    qs = to_sub(q).reshape(N, dil, nb, blk, A_KV_HEADS, G, HEAD_DIM)
    kb, vb = band(k), band(v)
    s = jnp.einsum('brnqkgd,brnskd->brnkgqs', qs, kb) * HEAD_DIM ** -0.5
    qi = jnp.arange(blk)[:, None]
    si = jnp.arange(2 * blk)[None, :]
    dist = qi + blk - si
    band_ok = (dist >= 0) & (dist <= n_back)
    first = (jnp.arange(nb)[:, None, None] == 0) & (si[None] < blk)
    ok = band_ok[None] & ~first
    s = jnp.where(ok[None, None, :, None, None], s, -jnp.inf)
    m = jnp.max(s, axis=-1, keepdims=True)
    e = jnp.exp(s - m)
    l = jnp.sum(e, axis=-1, keepdims=True)
    o = jnp.einsum('brnkgqs,brnskd->brnqkgd', e / l, vb)
    lse = (m + jnp.log(l))[..., 0]
    o = o.reshape(N, dil, s_pad // dil, A_HEADS, HEAD_DIM).swapaxes(1, 2).reshape(N, s_pad, A_HEADS, HEAD_DIM)[:, :S]
    lse = lse.transpose(0, 1, 2, 5, 3, 4).reshape(N, dil, s_pad // dil, A_HEADS).swapaxes(1, 2).reshape(N, s_pad, A_HEADS)[:, :S]
    return o, lse

def _dilated_sample(q, k_all, v_all, dil, n_back):
    f32 = jnp.float32
    N, T = q.shape[:2]
    G = A_HEADS // A_KV_HEADS
    lw = k_all.shape[1] - T
    idx = lw + jnp.arange(T)[:, None] - dil * jnp.arange(n_back + 1)[None, :]
    ok = idx >= 0
    idx = jnp.maximum(idx, 0)
    kg = k_all[:, idx].astype(f32)
    vg = v_all[:, idx].astype(f32)
    qg = q.astype(f32).reshape(N, T, A_KV_HEADS, G, HEAD_DIM)
    s = jnp.einsum('ntkgd,ntjkd->ntkgj', qg, kg) * HEAD_DIM ** -0.5
    s = jnp.where(ok[None, :, None, None, :], s, -jnp.inf)
    m = jnp.max(s, axis=-1, keepdims=True)
    e = jnp.exp(s - m)
    l = jnp.sum(e, axis=-1, keepdims=True)
    o = jnp.einsum('ntkgj,ntjkd->ntkgd', e / l, vg).reshape(N, T, A_HEADS, HEAD_DIM)
    lse = (m + jnp.log(l))[..., 0].reshape(N, T, A_HEADS)
    return o, lse

def _mix_dilations(results):
    o = jnp.stack([r[0] for r in results], axis=0)
    w = jax.nn.softmax(jnp.stack([r[1] for r in results], axis=0), axis=0)
    return jnp.sum(w[..., None] * o, axis=0)

def _dsa_attend(q, qi, wi, pos_q, k, v, ki, topk):
    f32 = jnp.float32
    N, T = q.shape[:2]
    L = k.shape[1]
    G = B_HEADS // B_KV_HEADS
    dots = jnp.einsum('nthd,nsd->ntsh', qi.astype(f32), ki.astype(f32)) * IDX_DIM ** -0.5
    score = jnp.einsum('ntsh,nth->nts', jax.nn.relu(dots), wi.astype(f32)) * IDX_HEADS ** -0.5
    admissible = jnp.arange(L)[None, :] <= pos_q[:, None]
    score = jnp.where(admissible[None], score, -jnp.inf)
    _, sel = lax.top_k(score, topk)
    sel_ok = sel <= pos_q[None, :, None]
    gather = jax.vmap(lambda a, i: a[i])
    kg = gather(k, sel).astype(f32)
    vg = gather(v, sel).astype(f32)
    qg = q.astype(f32).reshape(N, T, B_KV_HEADS, G, HEAD_DIM)
    s = jnp.einsum('ntkgd,ntjkd->ntkgj', qg, kg) * HEAD_DIM ** -0.5
    s = jnp.where(sel_ok[:, :, None, None, :], s, -jnp.inf)
    p = jax.nn.softmax(s, axis=-1)
    return jnp.einsum('ntkgj,ntjkd->ntkgd', p, vg).reshape(N, T, B_Q)

def _dsa_prompt(q, qi, wi, k, v, ki, topk):
    N, S = q.shape[:2]
    nblk = S // Q_BLOCK

    def blocks(a):
        return a.reshape(N, nblk, Q_BLOCK, *a.shape[2:]).swapaxes(0, 1)

    starts = jnp.arange(nblk, dtype=jnp.int32) * Q_BLOCK

    def one(args):
        qb, qib, wib, start = args
        return _dsa_attend(qb, qib, wib, start + jnp.arange(Q_BLOCK, dtype=jnp.int32), k, v, ki, topk)

    o = lax.map(one, (blocks(q), blocks(qi), blocks(wi), starts))
    return o.swapaxes(0, 1).reshape(N, S, B_Q)

def _mem_kv(mem, g_mem, w_mem_kv):
    N, M, _ = mem.shape
    mk, mv = jnp.split(_rmsnorm(mem, g_mem) @ w_mem_kv, 2, axis=-1)
    return mk.reshape(N, M, C_HEADS, HEAD_DIM), mv.reshape(N, M, C_HEADS, HEAD_DIM)

def _cross_attend(q, mk, mv):
    f32 = jnp.float32
    N, T = q.shape[:2]
    s = jnp.einsum('nthd,nmhd->nhtm', q.astype(f32), mk.astype(f32)) * HEAD_DIM ** -0.5
    p = jax.nn.softmax(s, axis=-1)
    return jnp.einsum('nhtm,nmhd->nthd', p, mv.astype(f32)).reshape(N, T, C_Q)

def _merge(x, oa, ag, ob, bg, oc, cg, w_out):
    N, T, _ = x.shape
    f32 = jnp.float32
    gated = lambda o, g: o.reshape(N, T, -1) * jax.nn.silu(g.astype(f32))
    mix = jnp.concatenate([gated(oa, ag), gated(ob, bg), gated(oc, cg)], axis=-1).astype(x.dtype)
    return x + mix @ w_out

def _gather_pages(pool, page_table):
    g = pool[page_table]
    return g.reshape(page_table.shape[0], page_table.shape[1] * pool.shape[1], *pool.shape[2:])

def setup_inputs(seed: int = 0) -> dict:
    key = jax.random.key(seed)
    ks = jax.random.split(key, 20)
    f32 = jnp.float32
    n_pages = PAST_LEN // PAGE_SIZE
    n_phys = (DEC_BATCH * n_pages * 5) // 4
    lw = min(WIN_MAX, PAST_LEN)
    nrm = lambda k, shape, scale=1.0: jax.random.normal(k, shape, f32) * scale
    page_table = jax.random.permutation(ks[10], n_phys)[: DEC_BATCH * n_pages].reshape(DEC_BATCH, n_pages).astype(jnp.int32)
    return {
        'x_prompt': nrm(ks[0], (BATCH, SEQ, D_MODEL)),
        'x_sample': nrm(ks[1], (DEC_BATCH, DEC_SEQ, D_MODEL)),
        'mem_prompt': nrm(ks[2], (BATCH, MEM_LEN, D_MODEL)),
        'cache_win_k': nrm(ks[3], (DEPTH, DEC_BATCH, lw, A_KV_HEADS, HEAD_DIM)),
        'cache_win_v': nrm(ks[4], (DEPTH, DEC_BATCH, lw, A_KV_HEADS, HEAD_DIM)),
        'cache_dsa_k': nrm(ks[5], (DEPTH, n_phys, PAGE_SIZE, B_KV_HEADS, HEAD_DIM)),
        'cache_dsa_v': nrm(ks[6], (DEPTH, n_phys, PAGE_SIZE, B_KV_HEADS, HEAD_DIM)),
        'cache_idx_k': nrm(ks[7], (DEPTH, n_phys, PAGE_SIZE, IDX_DIM)),
        'cache_mem_k': nrm(ks[8], (DEPTH, DEC_BATCH, MEM_LEN, C_HEADS, HEAD_DIM)),
        'cache_mem_v': nrm(ks[9], (DEPTH, DEC_BATCH, MEM_LEN, C_HEADS, HEAD_DIM)),
        'page_table': page_table,
        'g_in': 1.0 + nrm(ks[11], (DEPTH, D_MODEL), 0.01),
        'w_in': nrm(ks[12], (DEPTH, D_MODEL, IN_WIDTH), D_MODEL ** -0.5),
        'w_out': nrm(ks[13], (DEPTH, MIX_WIDTH, D_MODEL), MIX_WIDTH ** -0.5),
        'g_mem': 1.0 + nrm(ks[14], (DEPTH, D_MODEL), 0.01),
        'w_mem_kv': nrm(ks[15], (DEPTH, D_MODEL, 2 * C_Q), D_MODEL ** -0.5),
        'g_final': 1.0 + nrm(ks[16], (D_MODEL,), 0.01),
    }

def reference(x_prompt, x_sample, mem_prompt, cache_win_k, cache_win_v, cache_dsa_k, cache_dsa_v, cache_idx_k,
              cache_mem_k, cache_mem_v, page_table, g_in, w_in, w_out, g_mem, w_mem_kv, g_final):
    S = x_prompt.shape[1]
    T = x_sample.shape[1]
    past = page_table.shape[1] * cache_dsa_k.shape[2]
    pos_p = jnp.arange(S, dtype=jnp.int32)
    pos_s = past + jnp.arange(T, dtype=jnp.int32)
    keep = min(WIN_MAX, S)
    topk_p = min(TOPK_MAX, S // 4)
    topk_s = min(TOPK_MAX, (past + T) // 4)
    wkp, wvp, wks, wvs, dkp, dvp, ikp, dks, dvs, iks, mkp, mvp = ([] for _ in range(12))
    hp, hs = x_prompt, x_sample
    for l in range(DEPTH):
        aq, ak, av, ag, bq, bk, bv, iq, ik, iw, bg, cq, cg = _branch_inputs(hp, pos_p, g_in[l], w_in[l])
        oa = _mix_dilations([_dilated_prompt(aq, ak, av, d, w // d) for w, d in DILATED_PATTERNS])
        ob = _dsa_prompt(bq, iq, iw, bk, bv, ik, topk_p)
        mk, mv = _mem_kv(mem_prompt, g_mem[l], w_mem_kv[l])
        oc = _cross_attend(cq, mk, mv)
        hp = _merge(hp, oa, ag, ob, bg, oc, cg, w_out[l])
        wkp.append(ak[:, S - keep:])
        wvp.append(av[:, S - keep:])
        dkp.append(bk)
        dvp.append(bv)
        ikp.append(ik)
        mkp.append(mk)
        mvp.append(mv)
        aq, ak, av, ag, bq, bk, bv, iq, ik, iw, bg, cq, cg = _branch_inputs(hs, pos_s, g_in[l], w_in[l])
        ka = jnp.concatenate([cache_win_k[l], ak], axis=1)
        va = jnp.concatenate([cache_win_v[l], av], axis=1)
        oa = _mix_dilations([_dilated_sample(aq, ka, va, d, w // d) for w, d in DILATED_PATTERNS])
        kb_all = jnp.concatenate([_gather_pages(cache_dsa_k[l], page_table), bk], axis=1)
        vb_all = jnp.concatenate([_gather_pages(cache_dsa_v[l], page_table), bv], axis=1)
        ki_all = jnp.concatenate([_gather_pages(cache_idx_k[l], page_table), ik], axis=1)
        ob = _dsa_attend(bq, iq, iw, pos_s, kb_all, vb_all, ki_all, topk_s)
        oc = _cross_attend(cq, cache_mem_k[l], cache_mem_v[l])
        hs = _merge(hs, oa, ag, ob, bg, oc, cg, w_out[l])
        wks.append(ak)
        wvs.append(av)
        dks.append(bk)
        dvs.append(bv)
        iks.append(ik)
    y_prompt = _rmsnorm(hp, g_final)
    y_sample = _rmsnorm(hs, g_final)
    return (y_prompt, y_sample,
            jnp.stack(wkp, 0), jnp.stack(wvp, 0), jnp.stack(wks, 0), jnp.stack(wvs, 0),
            jnp.stack(dkp, 0), jnp.stack(dvp, 0), jnp.stack(ikp, 0),
            jnp.stack(dks, 0), jnp.stack(dvs, 0), jnp.stack(iks, 0),
            jnp.stack(mkp, 0), jnp.stack(mvp, 0))


_drawn_inputs = setup_inputs


def setup_inputs(seed=0):
    import zlib

    import numpy as np

    out = dict(_drawn_inputs(seed))
    spreads = {}
    factors = {'g_in': 5.516, 'g_mem': 5.765, 'g_final': 5.715}
    for name, (base, spread) in spreads.items():
        noise = np.random.default_rng([zlib.crc32(name.encode()), seed]).standard_normal(out[name].shape)
        drawn = base * np.exp(spread * noise) if base else spread * noise
        out[name] = __import__('jax').numpy.asarray(drawn.astype(out[name].dtype))
    for name, factor in factors.items():
        out[name] = (out[name] * factor).astype(out[name].dtype)
    return out
```

```python
from contextlib import ExitStack

import numpy as np
import concourse.bass as bass
from concourse import mybir

F32 = mybir.dt.float32
BF16 = mybir.dt.bfloat16
U16 = mybir.dt.uint16
I32 = mybir.dt.int32
ALU = mybir.AluOpType
ACT = mybir.ActivationFunctionType
AX = mybir.AxisListType

P = 128
D = 1024
SEQ = 4096
NT = SEQ // P
NSEQ = 8
TDEC = 8
NDEC = NSEQ * TDEC
PAST = 1024
PAGE = 128
PAGES = PAST // PAGE
HD = 64
MEM = 256
EPS = 1e-6
TOPK = 256
KD = D // P
SCALE = HD ** -0.5
IDX_SCALE = HD ** -0.5 * 8 ** -0.5
NEG = -1.0e30
FAR = -3.0e38

AQ, AK, AV, AG, BQ, BK, BV, IQ, IK, IW, BG, CQ, CG, ZW = (
    0, 384, 512, 640, 1024, 1408, 1536, 1664, 2176, 2240, 2248, 2632, 2888, 3144)
ZCHUNKS = [(c, min(512, ZW - c)) for c in range(0, ZW, 512)]
NZ = len(ZCHUNKS)

T_IQ, T_AQ, T_BQ, T_CQ, T_AK, T_BK, T_IK, T_N = 0, 4, 7, 10, 12, 13, 14, 15
TW = T_N * P
ROT = 16
WINDOW = 2048
PATTERNS = ((128, 1), (512, 4), (2048, 16))


def project_memory(nc, ins, outs, scr):
    with ExitStack() as ctx:
        def sb(name, shape, dt=F32):
            return ctx.enter_context(nc.sbuf_tensor("m_" + name, shape, dt))

        def sem(name):
            return ctx.enter_context(nc.semaphore("m_" + name))

        w = sb("w", [P, KD, 512])
        g = sb("g", [P, KD])
        ident = sb("ident", [P, P])
        x = sb("x", [P, 2, D])
        junk = sb("junk", [P, 2, D])
        ssq, ms, sd, rstd = (sb(n, [P, 2]) for n in ("ssq", "ms", "sd", "rstd"))
        xT = sb("xT", [P, 2, KD, P])
        z = sb("z", [P, 2, 512])
        mT = sb("mT", [P, 2, 2, P])
        tr = [ctx.enter_context(nc.psum_tensor(f"m_tr{i}", [P, 4, P], F32)) for i in range(4)]
        zp = [ctx.enter_context(nc.psum_tensor(f"m_zp{i}", [P, 512], F32)) for i in range(2)]
        kp = [ctx.enter_context(nc.psum_tensor(f"m_kp{i}", [P, 2, P], F32)) for i in range(2)]
        loaded, w_scaled, squared, mean_done, root_done, rstd_done = (
            sem(n) for n in ("loaded", "w_scaled", "squared", "mean_done", "root_done", "rstd_done"))
        x_turned, xT_ready, z_ready, z_done, k_turned, kT_ready, stored = (
            sem(n) for n in ("x_turned", "xT_ready", "z_ready", "z_done", "k_turned", "kT_ready", "stored"))
        block = ctx.enter_context(nc.Block())

        @block.sync
        def _(sp):
            sp.dma_start(x[:, :, :], ins["mem_prompt"].rearrange("(t p) d -> p t d", p=P)).then_inc(loaded, 16)
            sp.dma_start(ident[:, :], ins["ident"]).then_inc(loaded, 16)
            sp.dma_start(w[:, :, :], ins["w_mem_kv"].rearrange("(k p) n -> p k n", p=P)).then_inc(loaded, 16)
            sp.dma_start(g[:, :], ins["g_mem"].rearrange("(k p) -> p k", p=P),
                         allow_slow_non_contiguous=True).then_inc(loaded, 16)
            for t in range(2):
                sp.wait_ge(z_done, t + 1)
                sp.dma_start(outs["mem_k"][t * P:(t + 1) * P, :], z[:, t, 0:256]).then_inc(stored, 16)
                sp.dma_start(outs["mem_v"][t * P:(t + 1) * P, :], z[:, t, 256:512]).then_inc(stored, 16)
            sp.wait_ge(kT_ready, 2)
            sp.dma_start(scr["mem_kT"], mT[:, :, :, :].rearrange("p h t n -> p (h t n)"))\
                .then_inc(stored, 16)
            sp.wait_ge(stored, 5 * 16)

        @block.scalar
        def _(act):
            act.wait_ge(loaded, 64)
            for t in range(2):
                act.activation(junk[:, t, :], x[:, t, :], ACT.Square, accum_out=ssq[:, t:t + 1]).then_inc(squared, 1)
            act.wait_ge(mean_done, 1)
            act.activation(sd[:, :], ms[:, :], ACT.Sqrt).then_inc(root_done, 1)
            act.wait_ge(rstd_done, 1)
            for t in range(2):
                act.wait_ge(z_ready, t + 1)
                act.activation(z[:, t, :], zp[t][:, :], ACT.Copy, scale=rstd[:, t:t + 1]).then_inc(z_done, 1)

        @block.vector
        def _(dve):
            dve.wait_ge(loaded, 64)
            for k in range(KD):
                dve.tensor_scalar(w[:, k, :], w[:, k, :], g[:, k:k + 1], None, ALU.mult).then_inc(w_scaled, 1)
            dve.wait_ge(squared, 2)
            dve.tensor_scalar(ms[:, :], ssq[:, :], 1.0 / D, EPS, ALU.mult, ALU.add).then_inc(mean_done, 1)
            dve.wait_ge(root_done, 1)
            dve.reciprocal(rstd[:, :], sd[:, :]).then_inc(rstd_done, 1)
            for t in range(2):
                for h in range(2):
                    dve.wait_ge(x_turned, 2 * t + h + 1)
                    dve.tensor_copy(xT[:, t, 4 * h:4 * h + 4, :], tr[2 * t + h][:, :, :]).then_inc(xT_ready, 1)
            for t in range(2):
                dve.wait_ge(k_turned, t + 1)
                dve.tensor_copy(mT[:, :, t, :], kp[t][:, :, :]).then_inc(kT_ready, 1)

        @block.tensor
        def _(pe):
            pe.wait_ge(loaded, 64)
            for t in range(2):
                for k in range(KD):
                    mm = pe.transpose(tr[2 * t + k // 4][:, k % 4, :], x[:, t, k * P:(k + 1) * P], ident[:, :])
                    if k % 4 == 3:
                        mm.then_inc(x_turned, 1)
            pe.wait_ge(w_scaled, KD)
            for t in range(2):
                pe.wait_ge(xT_ready, 2 * t + 2)
                for k in range(KD):
                    mm = pe.matmul(zp[t][:, :], xT[:, t, k, :], w[:, k, :], start=(k == 0), stop=(k == KD - 1))
                mm.then_inc(z_ready, 1)
            for t in range(2):
                pe.wait_ge(z_done, t + 1)
                for h in range(2):
                    mm = pe.transpose(kp[t][:, h, :], z[:, t, h * P:(h + 1) * P], ident[:, :])
                mm.then_inc(k_turned, 1)


def project_tokens(nc, ins, outs, scr):
    NLAST = NT // 2
    with ExitStack() as ctx:
        def sb(name, shape, dt=F32):
            return ctx.enter_context(nc.sbuf_tensor("t_" + name, shape, dt))

        def sem(name):
            return ctx.enter_context(nc.semaphore("t_" + name))

        w = sb("w", [P, KD, ZW])
        g = sb("g", [P, KD])
        ident = sb("ident", [P, P])
        rope = sb("rope", [P, NT + 1, 2 * ROT])
        x = sb("x", [P, 2, D])
        junk = sb("junk", [P, D])
        ssq, ms, sd, rstd = (sb(n, [P, 2]) for n in ("ssq", "ms", "sd", "rstd"))
        xT = sb("xT", [P, 2, KD, P])
        z = sb("z", [P, 2, ZW])
        turned_a = sb("turned_a", [P, 25, ROT])
        turned_b = sb("turned_b", [P, 25, ROT])
        cs = sb("cs", [P, 2, 2 * ROT])
        sig = sb("sig", [P, 2 * 384 + 256])
        packed = sb("packed", [P, 2, 7, P])
        qT = sb("qT", [P, 2, TW])
        xp = [ctx.enter_context(nc.psum_tensor(f"t_xp{i}", [P, 4, P], F32)) for i in range(2)]
        zp = [ctx.enter_context(nc.psum_tensor(f"t_zp{i}", [P, 512], F32)) for i in range(2)]
        tp = [ctx.enter_context(nc.psum_tensor(f"t_tp{i}", [P, 4, P], F32)) for i in range(2)]

        const_in, w_in_s = sem("const_in"), sem("w_in")
        x_in = [sem(f"x_in{p}") for p in range(2)]
        cs_done, w_scaled, squared, mean_done, root_done, rstd_done = (
            sem(n) for n in ("cs_done", "w_scaled", "squared", "mean_done", "root_done", "rstd_done"))
        x_turned, xT_ready, z_ready, z_out = (sem(n) for n in ("x_turned", "xT_ready", "z_ready", "z_out"))
        rope_step, roped, pairs_packed, z_turned, qT_ready = (
            sem(n) for n in ("rope_step", "roped", "pairs_packed", "z_turned", "qT_ready"))
        exp_done, gate_step, gated = (sem(n) for n in ("exp_done", "gate_step", "gated"))
        z_stored = [sem(f"z_stored{p}") for p in range(2)]
        qT_stored = [sem(f"qT_stored{p}") for p in range(2)]
        block = ctx.enter_context(nc.Block())

        def heads(p, a, n, b=None):
            if b is None:
                return z[:, p, a:a + n * HD].rearrange("q (h d) -> q h d", d=HD)[:, :, 0:ROT]
            both = z[:, p, a:a + 2 * (b - a)].rearrange("q (s r) -> q s r", s=2)[:, :, 0:n * HD]
            return both.rearrange("q s (h d) -> q s h d", d=HD)[:, :, :, 0:ROT]

        @block.sync
        def _(sp):
            def load(u, p, t, sample=False):
                src = ins["x_sample"] if sample else ins["x_prompt"][bass.ts(t, P), :]
                rows = NDEC if sample else P
                sp.dma_start(x[0:rows, p, :], src).then_inc(x_in[p], 16)

            def store(u, p, t, sample=False):
                rows = NDEC if sample else P
                sp.wait_ge(roped, 2 * u + p + 1)
                at = bass.ts(t, P)
                zz = z[0:rows, p, :]
                pieces = []
                if sample:
                    pieces += [(outs["win_k_s"], AK, 128), (outs["win_v_s"], AV, 128), (outs["dsa_k_s"], BK, 128),
                               (outs["dsa_v_s"], BV, 128), (outs["idx_k_s"], IK, 64)]
                else:
                    pieces += [(scr["akv"][at, :], AK, 256), (outs["dsa_k"][at, :], BK, 128),
                               (outs["dsa_v"][at, :], BV, 128), (outs["idx_k"][at, :], IK, 64)]
                sp.dma_start(scr["iw"][at, :], z[:, p, IW:IW + 8]).then_inc(z_stored[p], 16)
                for dst, c, n in pieces:
                    sp.dma_start(dst, zz[:, c:c + n]).then_inc(z_stored[p], 16)
                sp.wait_ge(qT_ready, 4 * (2 * u + p + 1))
                sp.dma_start(scr["qkT"][bass.ts(t, P), :], qT[:, p, :]).then_inc(qT_stored[p], 16)
                sp.wait_ge(gated, 2 * u + p + 1)
                for dst, c, n in ((0, AG, 384), (384, BG, 384), (768, CG, 256)):
                    sp.dma_start(scr["gate"][at, dst:dst + n], z[:, p, c:c + n]).then_inc(z_stored[p], 16)

            def step(u, p, t, ahead):
                if ahead is not None:
                    sp.wait_ge(x_turned, 4 * u + 2 * p + 2)
                    sp.wait_ge(squared, 2 * u + p + 1)
                    load(u, p, ahead, sample=isinstance(ahead, str))
                store(u, p, t)

            load(0, 0, 0)
            load(0, 1, 1)
            sp.dma_start(ident[:, :], ins["ident"]).then_inc(const_in, 16)
            sp.dma_start(g[:, :], ins["g_in"].rearrange("(k p) -> p k", p=P),
                         allow_slow_non_contiguous=True).then_inc(const_in, 16)
            sp.dma_start(rope[:, :, :], ins["rope"]).then_inc(const_in, 16)
            for k in range(KD):
                sp.dma_start(w[:, k, :], ins["w_in"][k * P:(k + 1) * P, :]).then_inc(w_in_s, 16)
            step(0, 0, 0, 2)
            step(0, 1, 1, 3)
            with sp.Fori(1, NLAST - 1) as u:
                step(u, 0, 2 * u, 2 * u + 2)
                step(u, 1, 2 * u + 1, 2 * u + 3)
            u = NLAST - 1
            step(u, 0, 2 * u, "sample")
            step(u, 1, 2 * u + 1, None)
            store(NLAST, 0, NT, sample=True)
            for p in range(2):
                sp.wait_ge(qT_stored[p], 16 * (NLAST + 1 - p))
            sp.wait_ge(z_stored[0], 16 * (8 * NLAST + 9))
            sp.wait_ge(z_stored[1], 16 * 8 * NLAST)

        @block.scalar
        def _(act):
            def square(u, p):
                act.wait_ge(x_in[p], 16 * (u + 1))
                act.activation(junk[:, :], x[:, p, :], ACT.Square, accum_out=ssq[:, p:p + 1]).then_inc(squared, 1)

            def root(u, p):
                act.wait_ge(mean_done, 2 * u + p + 1)
                act.activation(sd[:, p:p + 1], ms[:, p:p + 1], ACT.Sqrt).then_inc(root_done, 1)

            def out_chunks(u, p, lo, hi, start):
                for c in range(lo, hi):
                    a, n = ZCHUNKS[c]
                    act.wait_ge(z_ready, NZ * (2 * u + p) + c + 1)
                    if c == lo == 0:
                        act.wait_ge(rstd_done, 2 * u + p + 1)
                        if not start:
                            act.wait_ge(z_stored[p], 16 * 8 * u)
                            act.wait_ge(z_turned, 4 * (2 * u + p - 1))
                    act.activation(z[:, p, a:a + n], zp[(NZ * p + c) % 2][:, 0:n], ACT.Copy,
                                   scale=rstd[:, p:p + 1]).then_inc(z_out, 1)

            def exps(u, p):
                act.wait_ge(z_out, NZ * (2 * u + p + 1))
                if not (isinstance(u, int) and u == 0 and p == 0):
                    act.wait_ge(gated, 2 * u + p)
                for s, (a, n) in zip((0, 384, 768), ((AG, 384), (BG, 384), (CG, 256))):
                    act.activation(sig[:, s:s + n], z[:, p, a:a + n], ACT.Exp, scale=-1.0).then_inc(exp_done, 1)

            def pack(u, p):
                act.wait_ge(roped, 2 * u + p + 1)
                for i, a in ((0, AQ), (3, BQ)):
                    src = z[:, p, a:a + 6 * HD].rearrange("q (s h d) -> q h s d", s=2, h=3)
                    dst = packed[:, p, i:i + 3, :].rearrange("q h (s d) -> q h s d", s=2)
                    act.activation(dst, src, ACT.Copy).then_inc(pairs_packed, 1)
                for s in range(2):
                    act.activation(packed[:, p, 6, s * HD:(s + 1) * HD], z[:, p, IK:IK + HD], ACT.Copy)\
                        .then_inc(pairs_packed, 1)

            def step(u, p, start=False, prev=None, ahead=None):
                if ahead:
                    square(*ahead)
                out_chunks(u, p, 0, 2, start)
                if prev:
                    pack(*prev)
                    exps(*prev)
                out_chunks(u, p, 2, 4, start)
                if ahead:
                    root(*ahead)
                out_chunks(u, p, 4, NZ, start)

            square(0, 0)
            root(0, 0)
            step(0, 0, start=True, ahead=(0, 1))
            step(0, 1, start=True, prev=(0, 0), ahead=(1, 0))
            with act.Fori(1, NLAST) as u:
                step(u, 0, prev=(u - 1, 1), ahead=(u, 1))
                step(u, 1, prev=(u, 0), ahead=(u + 1, 0))
            step(NLAST, 0, prev=(NLAST - 1, 1))
            pack(NLAST, 0)
            exps(NLAST, 0)

        @block.vector
        def _(dve):
            def mean(u, p):
                dve.wait_ge(squared, 2 * u + p + 1)
                dve.tensor_scalar(ms[:, p:p + 1], ssq[:, p:p + 1], 1.0 / D, EPS, ALU.mult, ALU.add)\
                    .then_inc(mean_done, 1)

            def recip(u, p):
                dve.wait_ge(root_done, 2 * u + p + 1)
                dve.reciprocal(rstd[:, p:p + 1], sd[:, p:p + 1]).then_inc(rstd_done, 1)

            def x_out(u, p, start=False):
                for h in range(2):
                    dve.wait_ge(x_turned, 2 * (2 * u + p) + h + 1)
                    if h == 0 and not start:
                        dve.wait_ge(z_ready, NZ * (2 * u + p - 1))
                    dve.tensor_copy(xT[:, p, 4 * h:4 * h + 4, :], xp[h][:, :, :]).then_inc(xT_ready, 1)

            def rotate(u, p, t):
                dve.wait_ge(z_out, NZ * (2 * u + p + 1))
                dve.wait_ge(const_in, 48)
                dve.tensor_copy(cs[:, p, :], rope[:, bass.ds(t, 1), :]).then_inc(cs_done, 1)
                dve.wait_ge(cs_done, 2 * u + p + 1)
                for pair, part in ((True, 0), (False, 16)):
                    n = 16 if pair else 9
                    v = heads(p, AQ, 8, BQ) if pair else heads(p, IQ, 9)
                    ta, tb = turned_a[:, part:part + n, :], turned_b[:, part:part + n, :]
                    if pair:
                        ta, tb = (t_.rearrange("q (s h) d -> q s h d", s=2) for t_ in (ta, tb))
                    def trig(a, b):
                        c = cs[:, p, a:b].unsqueeze(1)
                        if pair:
                            c = c.unsqueeze(1)
                        return c.to_broadcast([P, 2, 8, b - a] if pair else [P, 9, b - a])
                    def cut(v, a, b):
                        return v[:, :, :, a:b] if pair else v[:, :, a:b]
                    dve.tensor_tensor(ta, v, trig(0, 16), ALU.mult)
                    dve.tensor_tensor(cut(tb, 0, 8), cut(v, 8, 16), trig(16, 24), ALU.mult)
                    last = dve.tensor_tensor(cut(tb, 8, 16), cut(v, 0, 8), trig(24, 32), ALU.mult)
                    last.then_inc(rope_step, 1)
                dve.wait_ge(rope_step, 2 * (2 * u + p + 1))
                dve.tensor_tensor(heads(p, AQ, 8, BQ), turned_a[:, 0:16, :].rearrange("q (s h) d -> q s h d", s=2),
                                  turned_b[:, 0:16, :].rearrange("q (s h) d -> q s h d", s=2), ALU.add)
                dve.tensor_tensor(heads(p, IQ, 9), turned_a[:, 16:25, :], turned_b[:, 16:25, :], ALU.add)
                dve.tensor_scalar(z[:, p, IW:IW + 8], z[:, p, IW:IW + 8], IDX_SCALE, None, ALU.mult)\
                    .then_inc(roped, 1)

            def qT_out(u, p, start=False):
                for i in range(4):
                    n = 4 if i < 3 else T_N - 12
                    dve.wait_ge(z_turned, 4 * (2 * u + p) + i + 1)
                    if i == 0 and not start:
                        dve.wait_ge(qT_stored[p], 16 * u)
                    dve.tensor_copy(qT[:, p, i * 512:i * 512 + n * P],
                                    tp[i % 2][:, 0:n, :].rearrange("q a b -> q (a b)")).then_inc(qT_ready, 1)

            def gates(u, p):
                dve.wait_ge(exp_done, 3 * (2 * u + p + 1))
                dve.tensor_scalar(sig[:, :], sig[:, :], 1.0, None, ALU.add).then_inc(gate_step, 1)
                dve.wait_ge(gate_step, 2 * (2 * u + p) + 1)
                dve.reciprocal(sig[:, :], sig[:, :]).then_inc(gate_step, 1)
                dve.wait_ge(gate_step, 2 * (2 * u + p) + 2)
                for s, (a, n) in zip((0, 384, 768), ((AG, 384), (BG, 384), (CG, 256))):
                    last = dve.tensor_tensor(z[:, p, a:a + n], z[:, p, a:a + n], sig[:, s:s + n], ALU.mult)
                last.then_inc(gated, 1)

            def step(prev=None, prev_t=None, ahead=None, start=False, x_start=False):
                if prev:
                    rotate(*prev, prev_t)
                if ahead:
                    mean(*ahead)
                if prev:
                    qT_out(*prev, start=start)
                if ahead:
                    recip(*ahead)
                    x_out(*ahead, start=x_start)
                if prev:
                    gates(*prev)

            dve.wait_ge(const_in, 48)
            mean(0, 0)
            recip(0, 0)
            x_out(0, 0, start=True)
            dve.wait_ge(w_in_s, 16 * KD)
            for k in range(KD):
                dve.tensor_scalar(w[:, k, :], w[:, k, :], g[:, k:k + 1], None, ALU.mult).then_inc(w_scaled, 1)
            step(ahead=(0, 1), x_start=True)
            step(prev=(0, 0), prev_t=0, ahead=(1, 0), start=True)
            step(prev=(0, 1), prev_t=1, ahead=(1, 1), start=True)
            with dve.Fori(1, NLAST - 1) as u:
                step(prev=(u, 0), prev_t=2 * u, ahead=(u + 1, 0))
                step(prev=(u, 1), prev_t=2 * u + 1, ahead=(u + 1, 1))
            u = NLAST - 1
            step(prev=(u, 0), prev_t=2 * u, ahead=(u + 1, 0))
            step(prev=(u, 1), prev_t=2 * u + 1)
            step(prev=(NLAST, 0), prev_t=NT)

        @block.tensor
        def _(pe):
            def turn_x(u, p, start=False):
                pe.wait_ge(x_in[p], 16 * (u + 1))
                for k in range(KD):
                    if k % 4 == 0 and not start:
                        pe.wait_ge(xT_ready, 2 * (2 * u + p) + k // 4 - 1)
                    mm = pe.transpose(xp[k // 4][:, k % 4, :], x[:, p, k * P:(k + 1) * P], ident[:, :])
                    if k % 4 == 3:
                        mm.then_inc(x_turned, 1)

            def turn_z(u, p, start=False):
                pe.wait_ge(roped, 2 * u + p + 1)
                pe.wait_ge(pairs_packed, 4 * (2 * u + p + 1))
                cols = [z[:, p, IQ + P * i:IQ + P * (i + 1)] for i in range(4)]
                cols += [packed[:, p, i, :] for i in range(6)]
                cols += [z[:, p, CQ + P * i:CQ + P * (i + 1)] for i in range(2)]
                cols += [z[:, p, AK:AK + P], z[:, p, BK:BK + P], packed[:, p, 6, :]]
                for i, c in enumerate(cols):
                    if i % 4 == 0 and not (start and i < 8):
                        pe.wait_ge(qT_ready, 4 * (2 * u + p) + i // 4 - 1)
                    mm = pe.transpose(tp[i // 4 % 2][:, i % 4, :], c, ident[:, :])
                    if i % 4 == 3 or i == T_N - 1:
                        mm.then_inc(z_turned, 1)

            def tile(u, p, prev=None, ahead=None, start=False, prev_start=False):
                pe.wait_ge(xT_ready, 2 * (2 * u + p) + 2)
                for c, (a, n) in enumerate(ZCHUNKS):
                    if c == 2 and prev:
                        turn_z(*prev, start=prev_start)
                    if c == 5 and ahead:
                        turn_x(*ahead)
                    if not (start and c < 2):
                        pe.wait_ge(z_out, NZ * (2 * u + p) + c - 1)
                    for k in range(KD):
                        mm = pe.matmul(zp[(NZ * p + c) % 2][:, 0:n], xT[:, p, k, :], w[:, k, a:a + n],
                                       start=(k == 0), stop=(k == KD - 1))
                    mm.then_inc(z_ready, 1)

            pe.wait_ge(const_in, 48)
            turn_x(0, 0, start=True)
            pe.wait_ge(w_scaled, KD)
            tile(0, 0, ahead=(0, 1), start=True)
            tile(0, 1, prev=(0, 0), ahead=(1, 0), prev_start=True)
            with pe.Fori(1, NLAST) as u:
                tile(u, 0, prev=(u - 1, 1), ahead=(u, 1))
                tile(u, 1, prev=(u, 0), ahead=(u + 1, 0))
            tile(NLAST, 0, prev=(NLAST - 1, 1))
            turn_z(NLAST, 0)


class Tally:

    def __init__(self, sem, credit, per, tiles):
        self.sem, self.credit, self.per = sem, credit, per
        self.base = [credit + sum(p * n for p, n in zip(per[:g], tiles[:g])) for g in range(len(per))]

    def at(self, g, j, k):
        if isinstance(j, int):
            return self.base[g] + j * self.per[g] + k
        return j * self.per[g] + (self.base[g] + k)


class Attend:

    def __init__(self, kind, head, chunks):
        self.kind, self.head, self.chunks = kind, head, chunks
        if kind == "C":
            self.slot, self.half, self.out = T_CQ + head // 2, head % 2, (12 + head) * HD
        else:
            self.slot, self.half = (T_AQ if kind == "A" else T_BQ) + head % 3, head // 3
            self.out = (head if kind == "A" else 6 + head) * HD


def spans(lo, hi):
    return [(c, min(512, hi - c)) for c in range(lo, hi, 512)]


STAGES = 6


class Group:

    def __init__(self, tiles, idx, b_chunks, a_chunks, kinds):
        self.tiles, self.idx = tiles, idx
        self.width = sum(w for _, w in idx)
        order = (0, 3, 1, 4, 2, 5)
        self.heads = []
        if "B" in kinds:
            self.heads += [Attend("B", h, b_chunks) for h in order]
        self.n_b = len(self.heads)
        a_heads = [Attend("A", h, a_chunks) for h in order] if "A" in kinds else []
        c_heads = [Attend("C", h, [(0, MEM)]) for h in range(4)] if "C" in kinds else []
        self.heads += c_heads + a_heads
        self.n_idx = 8 * len(idx)
        self.first = [0]
        for a in self.heads:
            self.first.append(self.first[-1] + len(a.chunks))
        self.n_att = self.first[-1]
        self.s_all = self.n_idx + self.n_att
        self.n_a = max([self.first[i + 1] for i, a in enumerate(self.heads) if a.kind == "A"], default=0)
        self.s_b = self.n_idx + self.first[self.n_b]
        self.tail = max(self.n_b, len(self.heads) - STAGES)

    def part(self, a, lo, hi, n):
        at = lambda k: n * (self.first[k] - self.first[lo]) // (self.first[hi] - self.first[lo])
        return (at(a), at(a + 1)) if lo <= a < hi else (0, 0)


FEW_ROUNDS, ROUNDS = 12, 24
ASKED = 6 + 3 * FEW_ROUNDS + 4
MORE = 1 + 3 * (ROUNDS - FEW_ROUNDS) + 4
LINKS = ASKED + 2 + MORE + 14


def attend(nc, tag, R, nseq, groups, io):
    tiles = [g.tiles for g in groups]
    W = max([g.width for g in groups] + [512])
    WB = max([sum(w for _, w in a.chunks) for g in groups for a in g.heads if a.kind == "B"] + [W])
    SW = max(sum(w for _, w in a.chunks) for g in groups for a in g.heads)
    topk = any(a.kind == "B" for g in groups for a in g.heads)
    lastw = io["causal_width"]
    ptw = R if nseq == 1 else nseq * (R // nseq * (nseq + 1))
    with ExitStack() as ctx:
        def sb(name, shape, dt=F32):
            return ctx.enter_context(nc.sbuf_tensor(f"{tag}_{name}", shape, dt))

        def tally(name, credit, per):
            return Tally(ctx.enter_context(nc.semaphore(f"{tag}_{name}")), credit, [per(g) for g in groups], tiles)

        io["open"](ctx, sb)
        ident, q_sb = io["ident"], io["q"]
        S = sb("S", [R, 2, SW])
        PT = sb("PT", [P, 2, 4, ptw])
        o_sb = sb("o", [R, D])
        mc = sb("mc", [R, 2, 8])
        mjunk = sb("mjunk", [R, 2, 8])
        negm = sb("negm", [R, 2])
        lsum = sb("lsum", [R, 2])
        linv = sb("linv", [R, 2])
        zero_bias = sb("zero_bias", [R, MEM])
        if topk:
            X = sb("X", [R, W])
            relu = sb("relu", [R, 4, 512])
            Y = sb("Y", [R, W])
            GE = Y[:, :].bitcast(BF16)[:, 0:W]
            GT = Y[:, :].bitcast(BF16)[:, W:2 * W]
            rank = sb("rank", [R, W], U16)
            biasB = sb("biasB", [R, WB], BF16)
            col = sb("col", [R, 24])
            undone = sb("undone", [1, 1], I32)
            wtab = sb("wtab", [R, ROUNDS + 1])
            pow2 = sb("pow2", [R, ROUNDS + 1])
            ranks = sb("ranks", [R, 8])
            top8 = sb("top8", [R, 8])
            pick = sb("pick", [R, 8])
        SC = [ctx.enter_context(nc.psum_tensor(f"{tag}_SC{i}", [P, 512], F32)) for i in range(4)]
        TP = [ctx.enter_context(nc.psum_tensor(f"{tag}_TP{i}", [P, 4, R], F32)) for i in range(2)]
        OP = [ctx.enter_context(nc.psum_tensor(f"{tag}_OP{i}", [P, 512], F32)) for i in range(2)]

        n_heads = lambda g: len(g.heads)
        n_att = lambda g: g.n_att
        s_ready = tally("s_ready", 1, lambda g: g.s_all)
        relu_ready = tally("relu_ready", 1, lambda g: g.n_idx)
        idx_added = tally("idx_added", 4, lambda g: g.n_idx)
        s_biased = tally("s_biased", 1, n_att)
        max_ready = tally("max_ready", 1, n_heads)
        exp_done = tally("exp_done", 1, n_heads)
        p_turned = tally("p_turned", 1, n_att)
        pT_ready = tally("pT_ready", 2, n_att)
        pv_done = tally("pv_done", 2, n_att)
        inv_ready = tally("inv_ready", 1, n_heads)
        o_out = tally("o_out", 2, n_heads)
        step = tally("step", 1, lambda g: LINKS if g.idx else 0)
        q_in = tally("q_in", 16, lambda g: 32 if g.idx else 0)
        ac_in = tally("ac_in", 16, lambda g: 64 if g.n_att > g.first[g.n_b] else 0)
        b_in = tally("b_in", 16, lambda g: 32 if g.n_b else 0)
        bias_in = tally("bias_in", 16, lambda g: 16 if g.n_a else 0)
        causal_in = tally("causal_in", 16, lambda g: 16 if g.idx else 0)
        iw_in = tally("iw_in", 16, lambda g: 16 if g.idx else 0)
        o_stored = tally("o_stored", 16, lambda g: 32 if g.n_att > g.first[g.n_b] else 0)
        ob_stored = tally("ob_stored", 16, lambda g: 16 if g.n_b else 0)
        const_in = ctx.enter_context(nc.semaphore(f"{tag}_const_in"))
        keys_in = [ctx.enter_context(nc.semaphore(f"{tag}_keys_in{g}")) for g in range(len(groups) // 2 if io["n_keys"] else 0)]
        set_up = ctx.enter_context(nc.semaphore(f"{tag}_set_up"))
        passed = ctx.enter_context(nc.semaphore(f"{tag}_passed"))
        copied = ctx.enter_context(nc.semaphore(f"{tag}_copied"))
        sems = dict(s_ready=s_ready, s_biased=s_biased, idx_added=idx_added, step=step, q_in=q_in, ac_in=ac_in,
                    b_in=b_in, bias_in=bias_in, causal_in=causal_in, iw_in=iw_in, o_stored=o_stored, ob_stored=ob_stored, o_out=o_out,
                    const_in=const_in, keys_in=keys_in, copied=copied, passed=passed, set_up=set_up)
        block = ctx.enter_context(nc.Block())

        def wait(eng, t, g, j, k):
            eng.wait_ge(t.sem, t.at(g, j, k))

        def index_items(G):
            return [(2 * h2 + half, c0, w) for h2 in range(4) for c0, w in G.idx for half in range(2)]

        def over_tiles(eng, g, body):
            if groups[g].tiles == 1:
                body(g, 0)
            else:
                with eng.Fori(0, groups[g].tiles) as j:
                    body(g, j)

        RMIN, RMAX, RANGE, MID, MARGIN, CNT, STEP, HI, LO, KTH, RK, FEW, MANY, T1, CUT, C2, REST, FLOOR = range(18)

        @block.gpsimd
        def _(pool):
            for t in (s_ready, relu_ready, idx_added, s_biased, max_ready, exp_done, p_turned, pT_ready, pv_done,
                      inv_ready, o_out, step, q_in, ac_in, b_in, bias_in, causal_in, iw_in, o_stored, ob_stored):
                pool.sem_inc(t.sem, t.credit)
            pool.memset(zero_bias[:, :], 0.0).then_inc(set_up, 1)
            if nseq > 1:
                pool.memset(PT[:, :, :, :], 0.0).then_inc(set_up, 1)
            else:
                pool.memset(q_sb[:, :, :], 0.0).then_inc(set_up, 1)

        @block.sync
        def _(sp):
            if topk:
                sp.dma_start(pow2[:, :], io["pow2"][0:R, :]).then_inc(const_in, 16)
                sp.dma_start(ranks[:, :], io["ranks"][0:R, :]).then_inc(const_in, 16)
            else:
                sp.sem_inc(const_in, 32)
            io["sync"](sp, sems, o_sb)

        @block.tensor
        def _(pe):
            def bank_free(g, j, n):
                G = groups[g]
                m = n - 4
                if m < 0:
                    wait(pe, s_biased, g, j, 0)
                    if not groups[g - 1].heads:
                        wait(pe, relu_ready, g, j, 0)
                elif m < G.n_idx:
                    wait(pe, relu_ready, g, j, m + 1)
                else:
                    wait(pe, s_biased, g, j, m - G.n_idx + 1)

            def scores(kind, slot, half, c0, w, bank):
                for n in range(nseq):
                    mm = pe.matmul(bank[0:R, 0:w], io["query"](kind, slot, half, n), io["key"](kind, slot, half, n, c0, w),
                                   start=(n == 0), stop=(n == nseq - 1))
                mm.then_inc(s_ready.sem, 1)

            def head_scores(g, j, a):
                G = groups[g]
                A = G.heads[a]
                if a == G.n_b:
                    wait(pe, ac_in, g, j, 64)
                if a == 0 and G.n_b:
                    wait(pe, b_in, g, j, 32)
                for i, (c0, w) in enumerate(A.chunks):
                    n = G.n_idx + G.first[a] + i
                    bank_free(g, j, n)
                    scores(A.kind, A.slot, A.half, c0, w, SC[n % 4])

            def values(g, j, a, i):
                G = groups[g]
                A = G.heads[a]
                n = G.first[a] + i
                c0, w = A.chunks[i]
                if i == 0:
                    wait(pe, o_out, g, j, a - 1)
                wait(pe, pT_ready, g, j, n + 1)
                last_chunk = i == len(A.chunks) - 1
                for b in range(w // P):
                    for q in range(nseq):
                        lhs = PT[:, n % 2, b, q * R:(q + 1) * R] if nseq > 1 else PT[:, n % 2, b, :]
                        mm = pe.matmul(OP[a % 2][0:R, 0:HD], lhs, io["value"](A, q, c0 // P + b),
                                       start=(i == 0 and b == 0 and q == 0),
                                       stop=(last_chunk and b == w // P - 1 and q == nseq - 1))
                mm.then_inc(pv_done.sem, 1)

            def head_values(g, j, a):
                G = groups[g]
                A = G.heads[a]
                wait(pe, exp_done, g, j, a + 1)
                if G.idx and a == G.tail + 1:
                    wait(pe, step, g, j, ASKED + 2)
                    pe.sem_inc(passed, 1)
                for i, (c0, w) in enumerate(A.chunks):
                    n = G.first[a] + i
                    wait(pe, pT_ready, g, j, n - 1)
                    s0 = c0 - A.chunks[0][0]
                    for b in range(w // P):
                        mm = pe.transpose(TP[n % 2][:, b, :], S[:, a % 2, s0 + b * P:s0 + (b + 1) * P],
                                          ident[0:R, 0:R])
                    mm.then_inc(p_turned.sem, 1)
                    if i:
                        values(g, j, a, i - 1)
                values(g, j, a, len(A.chunks) - 1)

            def count_undone(g, j):
                wait(pe, step, g, j, ASKED)
                pe.matmul(TP[0][0:1, 0, 0:1], col[:, MANY:MANY + 1], col[:, MANY:MANY + 1], start=True, stop=True)\
                    .then_inc(step.sem, 1)

            def tile(g, j):
                G = groups[g]
                if G.n_idx:
                    wait(pe, q_in, g, j, 32)
                    for n, (h, c0, w) in enumerate(index_items(G)):
                        bank_free(g, j, n)
                        scores("I", T_IQ + h // 2, h % 2, c0, w, SC[n % 4])
                if G.heads:
                    head_scores(g, j, 0)
                elif G.idx:
                    count_undone(g, j)
                for a in range(len(G.heads)):
                    if a + 1 < len(G.heads):
                        head_scores(g, j, a + 1)
                    head_values(g, j, a)
                    if G.idx and a == G.tail:
                        count_undone(g, j)

            pe.wait_ge(const_in, io["n_const"])
            pe.wait_ge(set_up, io["n_set_up"])
            for g in range(len(groups)):
                if io["n_keys"] and g % 2 == 0 and g < len(groups) - 1:
                    pe.wait_ge(keys_in[g // 2], io["n_keys"])
                over_tiles(pe, g, tile)

        @block.scalar
        def _(act):
            def head(g, j, a):
                G = groups[g]
                A = G.heads[a]
                n_cols = sum(w for _, w in A.chunks)
                wait(act, max_ready, g, j, a + 1)
                act.activation(S[:, a % 2, 0:n_cols], S[:, a % 2, 0:n_cols], ACT.Exp, bias=negm[:, a % 2:a % 2 + 1],
                               accum_out=lsum[:, a % 2:a % 2 + 1]).then_inc(exp_done.sem, 1)
                for i, (c0, w) in enumerate(A.chunks):
                    n = G.first[a] + i
                    wait(act, pv_done, g, j, n - 1)
                    wait(act, p_turned, g, j, n + 1)
                    nb = w // P
                    if nseq == 1:
                        src, dst = TP[n % 2][:, 0:nb, :], PT[:, n % 2, 0:nb, :]
                    else:
                        src = TP[n % 2][:, 0:nb, :].rearrange("p b (n t) -> p b n t", n=nseq)
                        dst = PT[:, n % 2, 0:nb, :].rearrange("p b (n x) -> p b n x", n=nseq)[:, :, :, 0:R // nseq]
                    act.activation(dst, src, ACT.Copy).then_inc(pT_ready.sem, 1)

            def out(g, j, a):
                A = groups[g].heads[a]
                if a == 0 and groups[g].n_b:
                    wait(act, ob_stored, g, j, 0)
                if a == groups[g].n_b:
                    wait(act, o_stored, g, j, 0)
                wait(act, pv_done, g, j, groups[g].first[a + 1])
                wait(act, inv_ready, g, j, a + 1)
                act.activation(o_sb[:, A.out:A.out + HD], OP[a % 2][0:R, 0:HD], ACT.Copy,
                               scale=linv[:, a % 2:a % 2 + 1]).then_inc(o_out.sem, 1)

            def tile(g, j):
                G = groups[g]
                for n, (h, c0, w) in enumerate(index_items(G)):
                    wait(act, idx_added, g, j, n - 3)
                    wait(act, s_ready, g, j, n + 1)
                    act.activation(relu[:, n % 4, 0:w], SC[n % 4][0:R, 0:w], ACT.Relu).then_inc(relu_ready.sem, 1)
                for a in range(len(G.heads)):
                    head(g, j, a)
                    if a:
                        out(g, j, a - 1)
                if G.heads:
                    out(g, j, len(G.heads) - 1)

            for g in range(len(groups)):
                over_tiles(act, g, tile)

        @block.vector
        def _(dve):
            def c(i):
                return col[:, i:i + 1]

            def head(g, j, a):
                G = groups[g]
                A = G.heads[a]
                base = A.chunks[0][0]
                if a == G.n_b:
                    wait(dve, bias_in, g, j, 16)
                for i, (c0, w) in enumerate(A.chunks):
                    n = G.first[a] + i
                    if i == 0:
                        wait(dve, p_turned, g, j, G.first[a - 1] if a >= 2 else 0)
                    wait(dve, s_ready, g, j, G.n_idx + n + 1)
                    dve.sem_inc(passed, 1)
                    bias = {"A": io["biasA"], "B": biasB if topk else None, "C": zero_bias}[A.kind]
                    dve.tensor_tensor_reduce(S[:, a % 2, c0 - base:c0 - base + w], SC[(G.n_idx + n) % 4][0:R, 0:w],
                                             bias[:, c0 - base:c0 - base + w], SCALE, FAR, ALU.add, ALU.max,
                                             mc[:, a % 2, i:i + 1]).then_inc(s_biased.sem, 1)
                wait(dve, s_biased, g, j, G.first[a + 1])
                k = len(A.chunks)
                dve.tensor_scalar(mjunk[:, a % 2, 0:k], mc[:, a % 2, 0:k], -1.0, None, ALU.mult, ALU.min,
                                  accum_out=negm[:, a % 2:a % 2 + 1]).then_inc(max_ready.sem, 1)

            def inverse(g, j, a):
                wait(dve, exp_done, g, j, a + 1)
                if a >= 2:
                    wait(dve, o_out, g, j, a - 1)
                else:
                    wait(dve, o_out, g, j, 0)
                dve.reciprocal(linv[:, a % 2:a % 2 + 1], lsum[:, a % 2:a % 2 + 1]).then_inc(inv_ready.sem, 1)

            def tile(g, j):
                G = groups[g]
                nb, L = len(G.idx), G.width
                lk = [0]

                def link(ins):
                    lk[0] += 1
                    ins.then_inc(step.sem, 1)
                    wait(dve, step, g, j, lk[0])

                def index_scores():
                    wait(dve, iw_in, g, j, 16)
                    last = {}
                    for n, (h, c0, w) in enumerate(index_items(G)):
                        x, r = X[:, c0:c0 + w], relu[:, n % 4, 0:w]
                        wait(dve, relu_ready, g, j, n + 1)
                        if c0 not in last:
                            dve.tensor_scalar(x, r, io["iw"][:, 0:1], None, ALU.mult).then_inc(idx_added.sem, 1)
                        else:
                            wait(dve, idx_added, g, j, last[c0] + 1)
                            dve.scalar_tensor_tensor(x, r, io["iw"][:, h:h + 1], x, ALU.mult, ALU.add)\
                                .then_inc(idx_added.sem, 1)
                        last[c0] = n
                    wait(dve, idx_added, g, j, G.n_idx)

                def bracket():
                    link(dve.tensor_reduce(c(RMIN), X[:, 0:L], AX.X, ALU.min))
                    wait(dve, causal_in, g, j, 16)
                    link(dve.tensor_tensor(X[:, L - lastw:L], X[:, L - lastw:L], io["causal"], ALU.add))
                    link(dve.tensor_reduce(c(RMAX), X[:, 0:L], AX.X, ALU.max))
                    link(dve.tensor_tensor(c(RANGE), c(RMAX), c(RMIN), ALU.subtract))
                    dve.tensor_scalar(wtab[:, :], pow2[:, :], c(RANGE), None, ALU.mult)
                    dve.scalar_tensor_tensor(c(T1), c(RMIN), -1.0, c(RMAX), ALU.mult, ALU.max)
                    link(dve.scalar_tensor_tensor(c(MID), c(RANGE), 0.5, c(RMIN), ALU.mult, ALU.add))
                    margin(FEW_ROUNDS)

                def margin(n):
                    link(dve.scalar_tensor_tensor(c(MARGIN), c(T1), 2.0 ** -21, wtab[:, n:n + 1],
                                                  ALU.mult, ALU.add))

                def rounds(k0, k1):
                    for k in range(k0, k1):
                        link(dve.tensor_scalar(GE[:, 0:L], X[:, 0:L], c(MID), None, ALU.is_ge, ALU.add,
                                               accum_out=c(CNT)))
                        link(dve.tensor_scalar(c(STEP), c(CNT), float(TOPK), 0.5, ALU.is_ge, ALU.subtract))
                        link(dve.scalar_tensor_tensor(c(MID), c(STEP), wtab[:, k + 1:k + 2], c(MID),
                                                      ALU.mult, ALU.add))

                def count_above():
                    dve.tensor_tensor(c(HI), c(MID), c(MARGIN), ALU.add)
                    link(dve.tensor_tensor(c(LO), c(MID), c(MARGIN), ALU.subtract))
                    link(dve.tensor_scalar(GT[:, 0:L], X[:, 0:L], c(HI), None, ALU.is_gt, ALU.add, accum_out=c(CNT)))
                    link(dve.tensor_scalar(c(RK), c(CNT), -1.0, float(TOPK), ALU.mult, ALU.add))
                    link(dve.tensor_scalar(c(MANY), c(RK), 8.0, None, ALU.is_gt))

                def go_on():
                    assert lk[0] == ASKED, lk
                    lk[0] += 1
                    wait(dve, step, g, j, lk[0])
                    dve.sem_inc(passed, 1)
                    link(dve.tensor_copy(undone[:, :], TP[0][0:1, 0, 0:1]))
                    dve.sem_inc(passed, 1)
                    more = dve.value_load(undone[0:1, 0:1], min_val=0, max_val=R)
                    with dve.If(more > 0):
                        margin(ROUNDS)
                        rounds(FEW_ROUNDS, ROUNDS)
                        count_above()
                        dve.sem_inc(passed, 1)
                    with dve.Else():
                        dve.sem_inc(step.sem, MORE)
                    wait(dve, step, g, j, lk[0])

                def mask_above():
                    link(dve.tensor_scalar(Y[:, 0:L], X[:, 0:L], c(HI), FAR, ALU.is_gt, ALU.mult))
                    link(dve.tensor_tensor(Y[:, 0:L], Y[:, 0:L], X[:, 0:L], ALU.add))

                def pick_value():
                    dve.sem_inc(passed, 1)
                    link(dve.max(top8[:, :], Y[:, 0:L]))
                    dve.tensor_scalar(c(FEW), c(RK), 8.0, None, ALU.is_le)
                    link(dve.tensor_scalar(pick[:, :], ranks[:, :], c(RK), None, ALU.is_equal))
                    link(dve.tensor_tensor_reduce(pick[:, :], pick[:, :], top8[:, :], 1.0, 0.0, ALU.mult, ALU.add,
                                                  c(KTH)))
                    link(dve.tensor_tensor(c(KTH), c(KTH), c(FEW), ALU.mult))
                    dve.scalar_tensor_tensor(c(CUT), c(HI), c(MANY), c(KTH), ALU.mult, ALU.add)
                    link(dve.scalar_tensor_tensor(c(FLOOR), c(LO), c(MANY), c(KTH), ALU.mult, ALU.add))

                def compare():
                    dve.tensor_scalar(GT[:, 0:L], X[:, 0:L], c(CUT), None, ALU.is_gt, ALU.add, accum_out=c(C2))
                    link(dve.tensor_scalar(GE[:, 0:L], X[:, 0:L], c(FLOOR), None, ALU.is_ge))
                    link(dve.tensor_scalar(c(REST), c(C2), -1.0, float(TOPK), ALU.mult, ALU.add))

                def rank_equals():
                    link(dve.tensor_tensor_scan(rank[:, 0:L], GE[:, 0:L], GT[:, 0:L], 0.0, ALU.add, ALU.subtract))

                def choose():
                    link(dve.scalar_tensor_tensor(biasB[:, 0:L], rank[:, 0:L], c(REST), GT[:, 0:L],
                                                  ALU.is_le, ALU.max))

                def make_bias():
                    link(dve.tensor_tensor(biasB[:, 0:L], biasB[:, 0:L], GE[:, 0:L], ALU.mult))
                    link(dve.tensor_scalar(biasB[:, 0:L], biasB[:, 0:L], 1.0, -NEG, ALU.subtract, ALU.mult))
                    link(dve.tensor_tensor(biasB[:, L - lastw:L], biasB[:, L - lastw:L], io["causal"], ALU.add))
                    assert lk[0] == LINKS, lk

                if nb:
                    index_scores()
                n_heads = len(G.heads)
                tail = G.tail
                ends = ((count_above,), (go_on, mask_above), (pick_value,), (compare,), (rank_equals,),
                        (choose, make_bias))
                assert len(ends) == STAGES
                for a in range(n_heads):
                    head(g, j, a)
                    if a:
                        inverse(g, j, a - 1)
                    if nb and a == 0:
                        bracket()
                    elif nb and a < tail:
                        rounds(*G.part(a, 1, tail, FEW_ROUNDS))
                    elif nb:
                        for end in ends[a - tail]:
                            end()
                if n_heads:
                    inverse(g, j, n_heads - 1)
                elif nb:
                    bracket()
                    rounds(0, FEW_ROUNDS)
                    for end in sum(ends, ()):
                        end()

            dve.wait_ge(const_in, io["n_const"])
            dve.wait_ge(set_up, 2)
            for g in range(len(groups)):
                over_tiles(dve, g, tile)


def attend_prompt(nc, ins, outs, scr):
    NG, TG = NT // 4, 4
    upto = lambda g: spans(0, 512 * (g + 1))
    window = lambda g: spans(512 * max(0, g - 4), 512 * (g + 1))
    groups = []
    for g in range(NG):
        groups.append(Group(1, upto(g), upto(g - 1), window(g), "ABC" if g else "AC"))
        groups.append(Group(TG - 1, upto(g), upto(g), window(g), "ABC"))
    groups.append(Group(1, [], upto(NG - 1), [], "B"))
    t = {}
    S0 = WINDOW + 3 * P

    def opened(ctx, sb):
        for name, shape in (("akT", [P, SEQ]), ("bkT", [P, SEQ]), ("ikT", [P, SEQ]), ("av", [P, NT, P]),
                            ("bv", [P, NT, P]), ("ckT", [P, 2, MEM]), ("cv", [P, 2, MEM]), ("ident", [P, P]),
                            ("q", [P, 24, P]), ("iw", [P, 8]), ("biasA", [P, 5 * 512]), ("causal", [P, 512])):
            t[name] = sb(name, shape)
        io.update(ident=t["ident"], q=t["q"], biasA=t["biasA"], causal=t["causal"][:, :], iw=t["iw"])

    def key(kind, slot, half, n, c0, w):
        if kind == "C":
            return t["ckT"][:, slot - T_CQ, c0:c0 + w]
        return t[{"I": "ikT", "A": "akT", "B": "bkT"}[kind]][:, c0:c0 + w]

    def value(A, n, blk):
        if A.kind == "C":
            return t["cv"][:, blk, A.head * HD:(A.head + 1) * HD]
        return t["av" if A.kind == "A" else "bv"][:, blk, A.half * HD:(A.half + 1) * HD]

    def sync(sp, sems, o_sb):
        qkT = scr["qkT"]

        def load(which, g, j):
            rows = bass.ts(TG * g + j, P)

            def queries(lo, hi, sem):
                for half in range(2):
                    sp.dma_start(t["q"][HD * half:HD * half + HD, 2 * lo + half:2 * hi:2, :],
                                 qkT[bass.ds((TG * g + j) * P + HD * half, HD), lo * P:hi * P]
                                 .rearrange("p (s c) -> p s c", c=P)).then_inc(sems[sem].sem, 16)

            if which == "q":
                queries(T_IQ, T_AQ, "q_in")
            elif which == "iw":
                sp.dma_start(t["iw"][:, :], scr["iw"][rows, :]).then_inc(sems["iw_in"].sem, 16)
            elif which == "b":
                queries(T_BQ, T_CQ, "b_in")
            elif which == "ac":
                queries(T_AQ, T_BQ, "ac_in")
                queries(T_CQ, T_AK, "ac_in")
            elif which == "bias":
                n = 512 * min(g + 1, 5)
                off = S0 - (512 * min(g, 4) + j * P)
                sp.dma_start(t["biasA"][:, 0:n], ins["window"][:, bass.ds(off, n)]).then_inc(sems["bias_in"].sem, 16)
            elif which == "causal":
                sp.dma_start(t["causal"][:, :], ins["causal"][bass.ts(j, P), :]).then_inc(sems["causal_in"].sem, 16)

        def wait(name, g, j, k):
            sp.wait_ge(sems[name].sem, sems[name].at(g, j, k))

        def tile(s, j, four, jt, nxt):
            G = groups[s]
            if nxt:
                wait("s_ready", s, j, G.n_idx)
                load("q", *nxt)
                wait("idx_added", s, j, G.n_idx)
                load("iw", *nxt)
            if G.idx:
                if G.n_b:
                    wait("s_ready", s, j, G.s_b)
                load("b", four, jt)
            if G.n_b:
                wait("o_out", s, j, G.n_b)
                sp.dma_start(scr["o"][bass.ts(TG * four + jt - 1, P), 384:768], o_sb[:, 384:768])\
                    .then_inc(sems["ob_stored"].sem, 16)
            if nxt:
                wait("s_biased", s, j, G.n_a)
                sp.sem_inc(sems["passed"], 1)
                load("bias", *nxt)
                wait("s_ready", s, j, G.s_all)
                load("ac", *nxt)
            if G.idx:
                wait("o_out", s, j, len(G.heads))
                for a, b in ((0, 384), (768, 1024)):
                    sp.dma_start(scr["o"][bass.ts(TG * four + jt, P), a:b], o_sb[:, a:b])\
                        .then_inc(sems["o_stored"].sem, 16)
            if nxt:
                wait("step", s, j, LINKS)
                load("causal", *nxt)

        sp.wait_ge(sems["set_up"], 2)
        for which in ("q", "iw"):
            load(which, 0, 0)
        for name, src in (("ident", ins["ident"]), ("ckT", scr["mem_kT"].rearrange("p (h n) -> p h n", h=2)),
                          ("cv", outs["mem_v"].rearrange("(t p) c -> p t c", p=P))):
            dst = t[name][:, :] if name == "ident" else t[name][:, :, :]
            sp.dma_start(dst, src).then_inc(sems["const_in"], 16)
        for g in range(NG):
            rows = slice(512 * g, 512 * (g + 1))
            for name, src, c in (("ikT", qkT, T_IK * P), ("akT", qkT, T_AK * P), ("av", scr["akv"], P),
                                 ("bkT", qkT, T_BK * P), ("bv", outs["dsa_v"], 0)):
                view = src[rows, c:c + P].rearrange("(t p) c -> p t c", p=P)
                dst = (t[name][:, 4 * g:4 * g + 4, :] if name in ("av", "bv") else
                       t[name][:, rows].rearrange("p (t c) -> p t c", c=P))
                sp.dma_start(dst, view).then_inc(sems["keys_in"][g], 16)
            if g == 0:
                for which in ("ac", "bias", "causal"):
                    load(which, 0, 0)
        for i, name in enumerate(("win_k", "win_v")):
            sp.dma_start(outs[name], scr["akv"][SEQ - 2048:SEQ, i * P:(i + 1) * P]).then_inc(sems["copied"], 16)
        for g in range(NG):
            tile(2 * g, 0, g, 0, (g, 1))
            with sp.Fori(0, TG - 2) as j:
                tile(2 * g + 1, j, g, j + 1, (g, j + 2))
            tile(2 * g + 1, TG - 2, g, TG - 1, (g + 1, 0) if g + 1 < NG else None)
        tile(2 * NG, 0, NG, 0, None)
        sp.wait_ge(sems["copied"], 32)
        sp.wait_ge(sems["o_stored"].sem, 16 + 32 * NT)
        sp.wait_ge(sems["ob_stored"].sem, 16 + 16 * NT)

    io = {"open": opened, "query": lambda kind, slot, half, n: t["q"][:, 2 * slot + half, :],
          "key": key, "value": value, "sync": sync, "ident": None, "q": None,
          "pow2": ins["pow2"], "ranks": ins["ranks"], "n_const": 32 + 48, "n_set_up": 2, "n_keys": 80,
          "causal_width": 512}
    attend(nc, "p", P, 1, groups, io)


def attend_sampled(nc, ins, outs, scr, tag, kinds):
    R, KEYS = NDEC, PAST + P
    NB = KEYS // P
    paged = kinds == "B"
    keys = spans(0, KEYS)
    groups = [Group(1, keys, [], [], ""), Group(1, [], keys, [], "B")] if paged else [Group(1, [], [], keys, kinds)]
    DIAG = NSEQ * (R // NSEQ * (NSEQ + 1))
    with ExitStack() as ctx:
        def sb(name, shape, dt=F32):
            return ctx.enter_context(nc.sbuf_tensor(f"{tag}k_{name}", shape, dt))

        def sem(name):
            return ctx.enter_context(nc.semaphore(f"{tag}k_{name}"))

        kT = sb("kT", [P, NSEQ, KEYS])
        v = sb("v", [P, NSEQ, NB, P])
        kT2 = sb("kT2", [P, NSEQ, KEYS if paged else 512])
        v2 = None if paged else sb("v2", [P, NSEQ, 2, 256])
        ident = sb("ident", [P, P])
        q = sb("q", [P, 12, R])
        slots = [(T_IQ, T_AQ), (T_BQ, T_CQ)] if paged else [(T_AQ, T_BQ), (T_CQ, T_AK)]
        place = {lo: 0 if lo == slots[0][0] else slots[0][1] - slots[0][0] for lo, _ in slots}
        first = {"I": T_IQ, "A": T_AQ, "B": T_BQ, "C": T_CQ}
        qm = sb("qm", [P, 2 * sum(hi - lo for lo, hi in slots), DIAG])
        iw = sb("iw", [R, 8])
        causal = sb("causal", [R, P])
        biasA = sb("biasA", [R, KEYS])
        io = {"open": lambda c, s: None, "ident": ident, "q": q, "biasA": biasA, "causal": causal[:, :], "iw": iw,
              "query": lambda kind, slot, half, n: qm[:, 2 * (place[first[kind]] + slot - first[kind]) + half,
                                                       R * n:R * (n + 1)],
              "pow2": ins["pow2"], "ranks": ins["ranks"], "n_const": 32, "n_set_up": 2, "n_keys": 0,
              "causal_width": P}

        def key(kind, slot, half, n, c0, w):
            if kind == "C":
                return kT2[:, n, (slot - T_CQ) * MEM + c0:(slot - T_CQ) * MEM + c0 + w]
            return (kT2 if kind == "I" else kT)[:, n, c0:c0 + w]

        def value(A, n, blk):
            if A.kind == "C":
                return v2[:, n, blk, A.head * HD:(A.head + 1) * HD]
            return v[:, n, blk, A.half * HD:(A.half + 1) * HD]

        with ExitStack() as inner:
            nat = inner.enter_context(nc.sbuf_tensor(f"{tag}k_nat", [P, PAGES, P], F32))
            nat2 = inner.enter_context(nc.sbuf_tensor(f"{tag}k_nat2", [P, PAGES, P], F32))
            table = inner.enter_context(nc.sbuf_tensor(f"{tag}k_table", [1, NSEQ * PAGES], I32))
            NBANK = 4 if paged else 3
            tr = [inner.enter_context(nc.psum_tensor(f"{tag}k_tr{i}", [P, 512], F32)) for i in range(NBANK)]
            passed, cleared, once_in, table_in, loaded, turned, kT_ready, masked = (
                sem(n) for n in ("passed", "cleared", "once_in", "table_in", "loaded", "turned", "kT_ready", "masked"))
            block = inner.enter_context(nc.Block())

            def paged_rows(eng, n, b, names):
                page = eng.value_load(table[0:1, bass.ds(n * PAGES + b, 1)], min_val=0,
                                      max_val=ins["cache_idx_k"].shape[0] // PAGE - 1)
                return [ins[name][bass.ds(page * PAGE, PAGE), :] for name in names]

            def branch_loads(sp, n):
                if paged:
                    for b in range(PAGES):
                        k_rows, v_rows = paged_rows(sp, n, b, ("cache_dsa_k", "cache_dsa_v"))
                        sp.dma_start(nat[:, b, :], k_rows).then_inc(loaded, 16)
                        sp.dma_start(v[:, bass.ds(n, 1), b, :], v_rows.unsqueeze(1)).then_inc(loaded, 16)
                else:
                    rows = bass.ds(n * PAST, PAST)
                    sp.dma_start(nat[:, :, :], ins["cache_win_k"][rows, :].rearrange("(b p) c -> p b c", p=P))\
                        .then_inc(loaded, 16)
                    sp.dma_start(v[:, bass.ds(n, 1), 0:PAGES, :].rearrange("p n b c -> p (n b) c"),
                                 ins["cache_win_v"][rows, :].rearrange("(b p) c -> p b c", p=P))\
                        .then_inc(loaded, 16)

            def other_loads(act, n):
                if paged:
                    for b in range(PAGES):
                        rows, = paged_rows(act, n, b, ("cache_idx_k",))
                        for i in range(2):
                            act.dma_start(nat2[:, b, i * HD:(i + 1) * HD], rows).then_inc(loaded, 16)
                else:
                    mem = bass.ds(n * MEM, MEM)
                    act.dma_start(nat2[:, 0:4, :].rearrange("p (b h) c -> p b (h c)", b=2),
                                  ins["cache_mem_k"][mem, :].rearrange("(b p) c -> p b c", p=P))\
                        .then_inc(loaded, 16)
                    act.dma_start(v2[:, bass.ds(n, 1), :, :].rearrange("p n b c -> p (n b) c"),
                                  ins["cache_mem_v"][mem, :].rearrange("(b p) c -> p b c", p=P))\
                        .then_inc(loaded, 16)

            def over_sequences(eng, loads):
                loads(eng, 0)
                with eng.Fori(1, NSEQ) as n:
                    eng.wait_ge(turned, NBANK * n)
                    eng.sem_inc(passed, 1)
                    loads(eng, n)

            @block.gpsimd
            def _(pool):
                pool.memset(qm[:, :, :], 0.0).then_inc(cleared, 1)
                pool.memset(v[:, :, NB - 1, :], 0.0).then_inc(cleared, 1)
                pool.memset(kT[:, :, PAST:KEYS], 0.0).then_inc(cleared, 1)
                pool.memset(kT2[:, :, PAST:KEYS] if paged else v2[:, 0:1, 0, 0:1], 0.0).then_inc(cleared, 1)

            @block.sync
            def _(sp):
                new = scr["qkT"][SEQ:SEQ + P, :]
                sp.dma_start(ident[:, :], ins["ident"]).then_inc(once_in, 16)
                sp.dma_start(q[:, :, :], new[:, 0:12 * P].rearrange("p (s c) -> p s c", c=P)[:, :, 0:R])\
                    .then_inc(once_in, 16)
                sp.dma_start(table[:, :], ins["page_table"]).then_inc(table_in, 16)
                sp.wait_ge(cleared, 4)
                new_keys = [(kT, T_BK), (kT2, T_IK)] if paged else [(kT, T_AK)]
                for dst, slot in new_keys:
                    sp.dma_start(dst[:, :, PAST:PAST + TDEC],
                                 new[:, slot * P:slot * P + R].rearrange("p (n t) -> p n t", n=NSEQ))\
                        .then_inc(once_in, 16)
                sp.dma_start(v[0:TDEC, :, NB - 1, :],
                             outs["dsa_v_s" if paged else "win_v_s"].rearrange("(n t) c -> t n c", n=NSEQ))\
                    .then_inc(once_in, 16)
                sp.wait_ge(table_in, 16)
                over_sequences(sp, branch_loads)
                sp.wait_ge(once_in, 16 * (3 + len(new_keys)))

            @block.scalar
            def _(act):
                act.wait_ge(table_in, 16)
                act.wait_ge(cleared, 4)
                over_sequences(act, other_loads)

            LOADS = 16 * (4 * PAGES if paged else 4)

            @block.tensor
            def _(pe):
                def sequence(n, start):
                    pe.wait_ge(loaded, LOADS * (n + 1))
                    for i in range(4 * NBANK):
                        if i % 4 == 0 and not start:
                            pe.wait_ge(kT_ready, NBANK * (n - 1) + i // 4 + 1)
                        if i < 8:
                            src = nat[:, i, :]
                        elif paged:
                            src = nat2[:, i - 8, :]
                        else:
                            src = nat2[:, 2 * (i % 2) + (i - 8) // 2, :]
                        mm = pe.transpose(tr[i // 4][:, i % 4 * P:(i % 4 + 1) * P], src, ident[:, :])
                        if i % 4 == 3:
                            mm.then_inc(turned, 1)

                pe.wait_ge(once_in, 16 * (4 + paged))
                sequence(0, True)
                with pe.Fori(1, NSEQ) as n:
                    sequence(n, False)

            @block.vector
            def _(dve):
                dve.wait_ge(once_in, 16 * (4 + paged))
                dve.wait_ge(cleared, 4)
                for lo, hi in slots:
                    for half in range(2):
                        part = slice(HD * half, HD * half + HD)
                        dst = qm[part, 2 * place[lo] + half:2 * (place[lo] + hi - lo):2, :]
                        dve.tensor_copy(dst.rearrange("p s (n x) -> p s n x", n=NSEQ)[:, :, :, 0:TDEC],
                                        q[part, lo:hi, :].rearrange("p s (n t) -> p s n t", n=NSEQ))\
                            .then_inc(masked, 1)
                with dve.Fori(0, NSEQ) as n:
                    for b in range(NBANK):
                        dve.wait_ge(turned, NBANK * n + b + 1)
                        to, c = (kT, b * 512) if b < 2 else (kT2, (b - 2) * 512)
                        dve.tensor_copy(to[:, bass.ds(n, 1), c:c + 512].rearrange("p n c -> p (n c)"), tr[b][:, :])\
                            .then_inc(kT_ready, 1)

        def sync(sp, sems, o_sb):
            for name in ("q_in", "b_in") if paged else ("ac_in",):
                sp.sem_inc(sems[name].sem, 64)
            if paged:
                sp.dma_start(iw[:, :], scr["iw"][SEQ:SEQ + R, :]).then_inc(sems["iw_in"].sem, 16)
                sp.dma_start(causal[:, :], ins["causal_s"]).then_inc(sems["causal_in"].sem, 16)
            else:
                sp.dma_start(biasA[:, :], ins["window_s"]).then_inc(sems["bias_in"].sem, 16)
            last = len(groups) - 1
            sp.wait_ge(sems["o_out"].sem, sems["o_out"].at(last, 0, len(groups[last].heads)))
            for a, b in (((384, 768),) if paged else ((0, 384), (768, 1024))):
                sp.dma_start(scr["o"][SEQ:SEQ + R, a:b], o_sb[:, a:b]).then_inc(sems["copied"], 16)
            sp.wait_ge(sems["copied"], 16 if paged else 32)
            for name in ("iw_in", "causal_in") if paged else ("bias_in",):
                sp.wait_ge(sems[name].sem, 32)

        io.update(key=key, value=value, sync=sync)
        attend(nc, tag, R, NSEQ, groups, io)


def project_out(nc, ins, outs, scr):
    NLAST = NT // 2
    with ExitStack() as ctx:
        def sb(name, shape, dt=F32):
            return ctx.enter_context(nc.sbuf_tensor("f_" + name, shape, dt))

        def sem(name):
            return ctx.enter_context(nc.semaphore("f_" + name))

        w = sb("w", [P, KD, D])
        gf = sb("gf", [P, D])
        ident = sb("ident", [P, P])
        x, o, gate, mixT, h, y = (sb(n, [P, 2, D]) for n in ("x", "o", "gate", "mixT", "h", "y"))
        junk = sb("junk", [P, D])
        ssq, ms, sd, rstd = (sb(n, [P, 2]) for n in ("ssq", "ms", "sd", "rstd"))
        tp = [ctx.enter_context(nc.psum_tensor(f"f_tp{i}", [P, 512], F32)) for i in range(2)]
        zp = [ctx.enter_context(nc.psum_tensor(f"f_zp{i}", [P, 512], F32)) for i in range(4)]
        const_in = sem("const_in")
        og_in = [sem(f"og_in{p}") for p in range(2)]
        x_in = [sem(f"x_in{p}") for p in range(2)]
        stored = [sem(f"stored{p}") for p in range(2)]
        mixed, turned, mixT_ready, z_ready, h_ready, norm_act, norm_dve, y_ready = (
            sem(n) for n in ("mixed", "turned", "mixT_ready", "z_ready", "h_ready", "norm_act", "norm_dve",
                             "y_ready"))
        block = ctx.enter_context(nc.Block())

        def run(eng, body):
            body(0, 0, True)
            body(0, 1, True)
            with eng.Fori(1, NLAST) as u:
                body(u, 0, False)
                body(u, 1, False)
            body(NLAST, 0, False)

        @block.sync
        def _(sp):
            def load(u, p, start):
                last = isinstance(u, int) and u == NLAST
                rows, n = (slice(SEQ, SEQ + NDEC), NDEC) if last else (bass.ts(2 * u + p, P), P)
                if not start:
                    sp.wait_ge(turned, 4 * u + 2 * p - 2)
                sp.dma_start(o[0:n, p, :], scr["o"][rows, :]).then_inc(og_in[p], 16)
                sp.dma_start(gate[0:n, p, :], scr["gate"][rows, :]).then_inc(og_in[p], 16)
                if not start:
                    sp.wait_ge(h_ready, 4 * u + 2 * p - 2)
                src = ins["x_sample"] if last else ins["x_prompt"][rows, :]
                sp.dma_start(x[0:n, p, :], src).then_inc(x_in[p], 16)

            sp.dma_start(ident[:, :], ins["ident"]).then_inc(const_in, 16)
            load(0, 0, True)
            load(0, 1, True)
            for k in range(KD):
                sp.dma_start(w[:, k, :], ins["w_out"][k * P:(k + 1) * P, :]).then_inc(const_in, 16)
            sp.dma_start(gf[:, :], ins["g_final"].to_broadcast([P, D])).then_inc(const_in, 16)
            with sp.Fori(1, NLAST) as u:
                load(u, 0, False)
                load(u, 1, False)
            load(NLAST, 0, False)

        @block.gpsimd
        def _(pool):
            def store(u, p, start):
                last = isinstance(u, int) and u == NLAST
                pool.wait_ge(y_ready, 2 * u + p + 1)
                if last:
                    pool.dma_start(outs["y_s"], y[0:NDEC, p, :]).then_inc(stored[p], 16)
                else:
                    pool.dma_start(outs["y_p"][bass.ts(2 * u + p, P), :], y[:, p, :]).then_inc(stored[p], 16)

            run(pool, store)
            pool.wait_ge(stored[0], 16 * (NLAST + 1))
            pool.wait_ge(stored[1], 16 * NLAST)

        @block.vector
        def _(dve):
            def mix(u, p):
                dve.wait_ge(og_in[p], 32 * (u + 1))
                dve.tensor_tensor(o[:, p, :], o[:, p, :], gate[:, p, :], ALU.mult).then_inc(mixed, 1)

            def copy(u, p, start):
                for i in range(2):
                    dve.wait_ge(turned, 4 * u + 2 * p + i + 1)
                    if not start and i == 0:
                        dve.wait_ge(z_ready, 4 * u + 2 * p - 2)
                    dve.tensor_copy(mixT[:, p, i * 512:(i + 1) * 512], tp[i][:, :]).then_inc(mixT_ready, 1)

            def residual(u, p, start):
                dve.wait_ge(x_in[p], 16 * (u + 1))
                for i in range(2):
                    dve.wait_ge(z_ready, 4 * u + 2 * p + i + 1)
                    if not start and i == 0:
                        dve.wait_ge(norm_act, 6 * u + 3 * p - 3)
                    dve.tensor_tensor(h[:, p, i * 512:(i + 1) * 512], zp[2 * p + i][:, :],
                                      x[:, p, i * 512:(i + 1) * 512], ALU.add).then_inc(h_ready, 1)

            def norm(u, p):
                dve.wait_ge(norm_act, 6 * u + 3 * p + 1)
                dve.tensor_scalar(ms[:, p:p + 1], ssq[:, p:p + 1], 1.0 / D, EPS, ALU.mult, ALU.add)\
                    .then_inc(norm_dve, 1)
                dve.wait_ge(norm_act, 6 * u + 3 * p + 2)
                dve.reciprocal(rstd[:, p:p + 1], sd[:, p:p + 1]).then_inc(norm_dve, 1)
                dve.wait_ge(norm_act, 6 * u + 3 * p + 3)
                dve.tensor_tensor(y[:, p, :], y[:, p, :], gf[:, :], ALU.mult).then_inc(y_ready, 1)

            dve.wait_ge(const_in, 16 * (KD + 2))
            mix(0, 0)
            copy(0, 0, True)
            mix(0, 1)
            copy(0, 1, True)
            mix(1, 0)
            residual(0, 0, True)
            copy(1, 0, False)
            mix(1, 1)
            residual(0, 1, True)
            norm(0, 0)
            copy(1, 1, False)
            with dve.Fori(1, NLAST - 1) as u:
                mix(u + 1, 0)
                residual(u, 0, False)
                norm(u - 1, 1)
                copy(u + 1, 0, False)
                mix(u + 1, 1)
                residual(u, 1, False)
                norm(u, 0)
                copy(u + 1, 1, False)
            mix(NLAST, 0)
            residual(NLAST - 1, 0, False)
            norm(NLAST - 2, 1)
            copy(NLAST, 0, False)
            residual(NLAST - 1, 1, False)
            norm(NLAST - 1, 0)
            residual(NLAST, 0, False)
            norm(NLAST - 1, 1)
            norm(NLAST, 0)

        @block.scalar
        def _(act):
            def norm(u, p, start):
                act.wait_ge(h_ready, 4 * u + 2 * p + 2)
                act.activation(junk[:, :], h[:, p, :], ACT.Square, accum_out=ssq[:, p:p + 1]).then_inc(norm_act, 1)
                act.wait_ge(norm_dve, 4 * u + 2 * p + 1)
                act.activation(sd[:, p:p + 1], ms[:, p:p + 1], ACT.Sqrt).then_inc(norm_act, 1)
                if not start:
                    act.wait_ge(stored[p], 16 * u)
                act.wait_ge(norm_dve, 4 * u + 2 * p + 2)
                act.activation(y[:, p, :], h[:, p, :], ACT.Copy, scale=rstd[:, p:p + 1]).then_inc(norm_act, 1)

            run(act, norm)

        @block.tensor
        def _(pe):
            def turn(u, p, start):
                pe.wait_ge(mixed, 2 * u + p + 1)
                for k in range(KD):
                    if k % 4 == 0 and not start:
                        pe.wait_ge(mixT_ready, 4 * u + 2 * p - 1 + k // 4)
                    mm = pe.transpose(tp[k // 4][:, k % 4 * P:(k % 4 + 1) * P], o[:, p, k * P:(k + 1) * P],
                                      ident[:, :])
                    if k % 4 == 3:
                        mm.then_inc(turned, 1)

            def product(u, p, start):
                pe.wait_ge(mixT_ready, 4 * u + 2 * p + 2)
                for i in range(2):
                    if not start:
                        pe.wait_ge(h_ready, 4 * u + 2 * p - 3 + i)
                    for k in range(KD):
                        mm = pe.matmul(zp[2 * p + i][:, :], mixT[:, p, k * P:(k + 1) * P],
                                       w[:, k, i * 512:(i + 1) * 512], start=(k == 0), stop=(k == KD - 1))
                    mm.then_inc(z_ready, 1)

            pe.wait_ge(const_in, 16 * (KD + 2))
            turn(0, 0, True)
            turn(0, 1, False)
            product(0, 0, True)
            turn(1, 0, False)
            product(0, 1, True)
            turn(1, 1, False)
            with pe.Fori(1, NLAST - 1) as u:
                product(u, 0, False)
                turn(u + 1, 0, False)
                product(u, 1, False)
                turn(u + 1, 1, False)
            product(NLAST - 1, 0, False)
            turn(NLAST, 0, False)
            product(NLAST - 1, 1, False)
            product(NLAST, 0, False)


SCRATCH = {"mem_kT": (P, 2 * MEM), "akv": (SEQ, 256), "iw": ((NT + 1) * P, 8), "gate": ((NT + 1) * P, D),
           "qkT": ((NT + 1) * P, TW), "o": ((NT + 1) * P, D)}


def shape_tables():
    f = np.float32
    half = ROT // 2
    inv = np.power(f(500000.0), -np.arange(half, dtype=f) * f(2.0) / f(ROT)).astype(f)
    pos = np.concatenate([np.arange(SEQ), PAST + np.arange(NDEC) % TDEC, np.zeros(P - NDEC)]).astype(f)
    ang = pos[:, None] * inv[None, :]
    cos, sin = np.cos(ang).astype(f), np.sin(ang).astype(f)
    rope = np.concatenate([cos, cos, -sin, sin], axis=1).reshape(NT + 1, P, 2 * ROT).transpose(1, 0, 2)

    def weight(dist):
        c = sum(((dist >= 0) & (dist % d == 0) & (dist <= w)).astype(np.int64) for w, d in PATTERNS)
        return np.where(c > 0, np.log(np.maximum(c, 1)) / SCALE, NEG).astype(f)

    first = WINDOW + 3 * P
    window = weight(np.arange(P)[:, None] - np.arange(first + 512)[None, :] + first)
    u, t = np.arange(PAST + P)[None, :], (np.arange(NDEC) % TDEC)[:, None]
    window_s = np.where(u < PAST + TDEC, weight(PAST + t - u), f(NEG)).astype(f)
    causal = np.where(np.arange(512)[None, :] <= np.arange(512)[:, None], 0.0, NEG).astype(f)
    causal_s = np.where(np.arange(P)[None, :] <= t, 0.0, NEG).astype(f)
    pow2 = np.tile(2.0 ** -np.arange(ROUNDS + 1), (P, 1)).astype(f)
    ranks = np.tile(np.arange(1, 9), (P, 1)).astype(f)
    return {"ident": np.eye(P, dtype=f), "rope": rope, "window": window, "window_s": window_s,
            "causal": causal, "causal_s": causal_s, "pow2": pow2, "ranks": ranks}


def build(nc, ins, outs, scr):
    project_memory(nc, ins, outs, scr)
    project_tokens(nc, ins, outs, scr)
    attend_prompt(nc, ins, outs, scr)
    attend_sampled(nc, ins, outs, scr, "b", "B")
    attend_sampled(nc, ins, outs, scr, "a", "AC")
    project_out(nc, ins, outs, scr)


_OUTS = [("y_p", (SEQ, D)), ("y_s", (NDEC, D)),
         ("win_k", (2048, 128)), ("win_v", (2048, 128)), ("win_k_s", (NDEC, 128)), ("win_v_s", (NDEC, 128)),
         ("dsa_k", (SEQ, 128)), ("dsa_v", (SEQ, 128)), ("idx_k", (SEQ, HD)),
         ("dsa_k_s", (NDEC, 128)), ("dsa_v_s", (NDEC, 128)), ("idx_k_s", (NDEC, HD)),
         ("mem_k", (MEM, 256)), ("mem_v", (MEM, 256))]
_SHAPES = [(1, SEQ, D), (NSEQ, TDEC, D), (1, 1, 2048, 2, HD), (1, 1, 2048, 2, HD), (1, NSEQ, TDEC, 2, HD),
           (1, NSEQ, TDEC, 2, HD), (1, 1, SEQ, 2, HD), (1, 1, SEQ, 2, HD), (1, 1, SEQ, HD),
           (1, NSEQ, TDEC, 2, HD), (1, NSEQ, TDEC, 2, HD), (1, NSEQ, TDEC, HD),
           (1, 1, MEM, 4, HD), (1, 1, MEM, 4, HD)]


def kernel(**inputs):
    import numpy as _np
    import concourse.bacc as _bacc
    from concourse import mybir as _mybir
    from concourse.bass_utils import run_bass_kernel_spmd as _run

    nc = _bacc.Bacc("TRN2", target_bir_lowering=False, num_devices=1)
    views = {
        "x_prompt": (SEQ, D), "x_sample": (NDEC, D), "mem_prompt": (MEM, D),
        "cache_win_k": (NSEQ * PAST, 128), "cache_win_v": (NSEQ * PAST, 128),
        "cache_dsa_k": (-1, 128), "cache_dsa_v": (-1, 128), "cache_idx_k": (-1, HD),
        "cache_mem_k": (NSEQ * MEM, 256), "cache_mem_v": (NSEQ * MEM, 256),
        "page_table": (1, NSEQ * PAGES), "g_in": (D,), "w_in": (D, ZW), "w_out": (D, D), "g_mem": (D,),
        "w_mem_kv": (D, 512), "g_final": (1, D),
    }
    arrays, ins, outs, scr = {}, {}, {}, {}
    given = {name: _np.asarray(inputs[name]).reshape(shape) for name, shape in views.items()}
    given.update(shape_tables())
    for name, a in given.items():
        a = _np.ascontiguousarray(a)
        arrays[f"in_{name}"] = a
        ins[name] = nc.dram_tensor(f"in_{name}", a.shape, _mybir.dt.from_np(a.dtype), kind="ExternalInput").ap()
    for name, shape in _OUTS:
        outs[name] = nc.dram_tensor(f"out_{name}", shape, F32, kind="ExternalOutput").ap()
    for name, shape in SCRATCH.items():
        scr[name] = nc.dram_tensor(f"scr_{name}", shape, F32, kind="Internal").ap()
    build(nc, ins, outs, scr)
    r = _run(nc, [arrays], core_ids=[0])
    got = [r.results[0][f"out_{name}"] for name, _ in _OUTS]
    return tuple(_np.asarray(a).reshape(s) for a, s in zip(got, _SHAPES))
```
